# Optimizing a Trainium2 kernel written in Bass

```python
import jax, jax.numpy as jnp
from jax import lax
import numpy as np

D_MODEL = 1024
BATCH = 1
SEQ = 256
DEPTH = 2
DEC_BATCH = 8
DEC_SEQ = 1
PAST_LEN = 2048
PAGE_SIZE = 128

N_EVEN = (DEPTH + 1) // 2
N_ODD = DEPTH // 2

GLA_HEADS = 4
GLA_DV = D_MODEL // 2 // GLA_HEADS
GLA_DK = GLA_DV // 2
GLA_KW = GLA_HEADS * GLA_DK
GLA_VW = GLA_HEADS * GLA_DV
GLA_GATE_RANK = 16
GLA_TAU = 16.0
GLA_CHUNK = 16
CONV_CH = D_MODEL // 2
CONV_WIDTH = 31
IN0_SIZES = (GLA_KW, GLA_KW, GLA_VW, GLA_VW, GLA_GATE_RANK, 2 * CONV_CH)
IN0_WIDTH = sum(IN0_SIZES)
MIX0_WIDTH = GLA_VW + CONV_CH
POOL_WINDOWS = (2, 4, 8, 16)
POOL_GROUPS = len(POOL_WINDOWS)
POOL_GC = D_MODEL // POOL_GROUPS
POOL_BUF = max(POOL_WINDOWS) - 1
MOE_GROUPS = 4
MOE_EXPERTS = 4
MOE_TOPK = 2
MOE_FF = 512
ALPHA = (2 * DEPTH) ** 0.25
BETA = (8 * DEPTH) ** -0.25
LN_EPS = 1e-5

kernel_name = "hybrid_gla_conformer_pool_hmoe_step"

def _standardize(x):
    xf = x.astype(jnp.float32)
    mu = jnp.mean(xf, -1, keepdims=True)
    var = jnp.mean(jnp.square(xf - mu), -1, keepdims=True)
    return ((xf - mu) * lax.rsqrt(var + LN_EPS)).astype(x.dtype)

def layer_norm(x, gain, bias):
    return _standardize(x) * gain + bias

def ada_mod(c, w, b):
    m = jax.nn.silu(c) @ w + b
    shift, scale, gate = jnp.split(m, 3, axis=-1)
    return shift[:, None], scale[:, None], gate[:, None]

def gla_recurrence(q, k, v, log_a, s0):
    B, L = q.shape[:2]
    C = min(GLA_CHUNK, L)
    pad = (-L) % C
    f32 = jnp.float32
    q, k, v, log_a = (t.astype(f32) for t in (q, k, v, log_a))
    if pad:
        pw = ((0, 0), (0, pad), (0, 0), (0, 0))
        q, k, v, log_a = (jnp.pad(t, pw) for t in (q, k, v, log_a))
    n = (L + pad) // C

    def to_chunks(t):
        return t.reshape(B, n, C, GLA_HEADS, t.shape[-1]).transpose(1, 0, 3, 2, 4)

    mask = jnp.tril(jnp.ones((C, C), dtype=bool))[:, :, None]

    def step(s, inp):
        qc, kc, vc, ac = inp
        b = jnp.cumsum(ac, axis=2)
        o_inter = jnp.einsum('bhck,bhkv->bhcv', qc * jnp.exp(b), s)
        diff = b[:, :, :, None, :] - b[:, :, None, :, :]
        dec = jnp.where(mask, jnp.exp(jnp.where(mask, diff, 0.0)), 0.0)
        att = jnp.einsum('bhtk,bhsk,bhtsk->bhts', qc, kc, dec)
        o_intra = jnp.einsum('bhts,bhsv->bhtv', att, vc)
        b_last = b[:, :, -1]
        s_new = jnp.exp(b_last)[..., None] * s + jnp.einsum(
            'bhsk,bhsv->bhkv', kc * jnp.exp(b_last[:, :, None] - b), vc)
        return s_new, o_inter + o_intra

    s_fin, o = lax.scan(step, s0.astype(f32),
                        (to_chunks(q), to_chunks(k), to_chunks(v), to_chunks(log_a)))
    o = o.transpose(1, 0, 3, 2, 4).reshape(B, n * C, GLA_HEADS, GLA_DV)[:, :L]
    return o, s_fin.astype(s0.dtype)

def mixer_even(h, s_gla, conv_buf, w_in, w_a2, b_a, gla_norm_g, conv_w, conv_b,
               conv_ln_g, conv_ln_b, w_out):
    B, L, _ = h.shape
    z = h @ w_in
    q, k, v, g, a_lr, u = jnp.split(z, np.cumsum(IN0_SIZES)[:-1].tolist(), axis=-1)
    q = q.reshape(B, L, GLA_HEADS, GLA_DK) * (GLA_DK ** -0.5)
    k = k.reshape(B, L, GLA_HEADS, GLA_DK)
    v = v.reshape(B, L, GLA_HEADS, GLA_DV)
    log_a = jax.nn.log_sigmoid((a_lr @ w_a2 + b_a).astype(jnp.float32)) / GLA_TAU
    log_a = log_a.reshape(B, L, GLA_HEADS, GLA_DK)
    o, s_new = gla_recurrence(q, k, v, log_a, s_gla)
    o = _standardize(o.astype(h.dtype)).reshape(B, L, GLA_VW) * gla_norm_g
    o = o * jax.nn.silu(g)
    ua, ug = jnp.split(u, 2, axis=-1)
    glu = ua * jax.nn.sigmoid(ug)
    full = jnp.concatenate([conv_buf.astype(glu.dtype), glu], axis=1)
    y = lax.conv_general_dilated(full, conv_w[:, None, :].astype(full.dtype), window_strides=(1,),
                                 padding='VALID', dimension_numbers=('NWC', 'WIO', 'NWC'),
                                 feature_group_count=CONV_CH) + conv_b
    y = jax.nn.silu(layer_norm(y, conv_ln_g, conv_ln_b))
    new_buf = full[:, -(CONV_WIDTH - 1):]
    return jnp.concatenate([o, y], axis=-1) @ w_out, s_new, new_buf

def mixer_odd(h, pool_buf, start_pos, w_grp, pool_scale, w_out):
    B, L, D = h.shape
    full = jnp.concatenate([pool_buf.astype(h.dtype), h], axis=1)
    cs = jnp.cumsum(full.astype(jnp.float32), axis=1)
    cs = jnp.concatenate([jnp.zeros((B, 1, D), jnp.float32), cs], axis=1)
    end = cs[:, POOL_BUF + 1:]
    pos = start_pos + jnp.arange(L)
    outs = []
    for gi, w in enumerate(POOL_WINDOWS):
        sl = slice(gi * POOL_GC, (gi + 1) * POOL_GC)
        start = cs[:, POOL_BUF + 1 - w: POOL_BUF + 1 - w + L, sl]
        cnt = jnp.minimum(w, pos + 1).astype(jnp.float32)[None, :, None]
        outs.append((end[..., sl] - start) / cnt)
    pooled = jnp.concatenate(outs, axis=-1).astype(h.dtype) - h
    mixed = jnp.einsum('blgc,gcd->blgd', pooled.reshape(B, L, POOL_GROUPS, POOL_GC), w_grp)
    mixed = mixed.reshape(B, L, D) * pool_scale
    return mixed @ w_out, full[:, -POOL_BUF:]

def hier_moe(h, w_coarse, b_coarse, w_fine, b_fine, w_gate, w_up, w_down):
    B, L, D = h.shape
    t = h.reshape(-1, D)
    pc = jax.nn.softmax((t @ w_coarse + b_coarse).astype(jnp.float32), axis=-1)
    pg, gidx = lax.top_k(pc, 1)
    fine_logits = jnp.einsum('td,gde->tge', t, w_fine) + b_fine
    fine_sel = jnp.take_along_axis(fine_logits, gidx[:, :, None], axis=1)[:, 0]
    pf = jax.nn.softmax(fine_sel.astype(jnp.float32), axis=-1)
    vals, eidx = lax.top_k(pf, MOE_TOPK)
    wts = pg * (vals / jnp.sum(vals, -1, keepdims=True))
    fine_w = jnp.sum(jax.nn.one_hot(eidx, MOE_EXPERTS) * wts[..., None], axis=1)
    comb = (jax.nn.one_hot(gidx[:, 0], MOE_GROUPS)[:, :, None] * fine_w[:, None, :]).astype(t.dtype)
    out = jnp.zeros_like(t)
    for g in range(MOE_GROUPS):
        hid = jax.nn.silu(jnp.einsum('td,edf->tef', t, w_gate[g])) * jnp.einsum('td,edf->tef', t, w_up[g])
        out = out + jnp.einsum('tef,efd->td', hid * comb[:, g, :, None], w_down[g])
    return out.reshape(B, L, D)

def trunk(x, c, s_gla, s_conv, s_pool, start_pos, p):
    new_gla, new_conv, new_pool = [], [], []
    for layer in range(DEPTH):
        i = layer // 2
        shift, scale, gate = ada_mod(c, p['w_ada'][layer, 0], p['b_ada'][layer, 0])
        h = x * (1 + scale) + shift
        if layer % 2 == 0:
            m, sg, sc = mixer_even(h, s_gla[i], s_conv[i], p['w_in_even'][i], p['w_a2'][i], p['b_a'][i],
                                   p['gla_norm_g'][i], p['conv_w'][i], p['conv_b'][i], p['conv_ln_g'][i],
                                   p['conv_ln_b'][i], p['w_out_even'][i])
            new_gla.append(sg)
            new_conv.append(sc)
        else:
            m, sp = mixer_odd(h, s_pool[i], start_pos, p['w_grp_pool'][i], p['pool_scale'][i],
                              p['w_out_odd'][i])
            new_pool.append(sp)
        x = layer_norm(ALPHA * x + (1 + gate) * m, p['ln_g'][layer, 0], p['ln_b'][layer, 0])
        shift, scale, gate = ada_mod(c, p['w_ada'][layer, 1], p['b_ada'][layer, 1])
        h = x * (1 + scale) + shift
        m = hier_moe(h, p['w_coarse'][layer], p['b_coarse'][layer], p['w_fine'][layer], p['b_fine'][layer],
                     p['w_gate'][layer], p['w_up'][layer], p['w_down'][layer])
        x = layer_norm(ALPHA * x + (1 + gate) * m, p['ln_g'][layer, 1], p['ln_b'][layer, 1])
    return x, jnp.stack(new_gla), jnp.stack(new_conv), jnp.stack(new_pool)

def setup_inputs(seed: int = 0) -> dict:
    key = jax.random.key(seed)
    ks = iter(jax.random.split(key, 40))
    nrm = lambda shape, s: jax.random.normal(next(ks), shape, jnp.float32) * s
    D = D_MODEL
    return {
        "x_prompt": nrm((BATCH, SEQ, D), 1.0),
        "x_sample": nrm((DEC_BATCH, DEC_SEQ, D), 1.0),
        "state_gla": nrm((N_EVEN, DEC_BATCH, GLA_HEADS, GLA_DK, GLA_DV), 1.0),
        "state_conv": nrm((N_EVEN, DEC_BATCH, CONV_WIDTH - 1, CONV_CH), 0.5),
        "state_pool": nrm((N_ODD, DEC_BATCH, POOL_BUF, D), 1.0),
        "c_prompt": nrm((BATCH, D), 1.0),
        "c_sample": nrm((DEC_BATCH, D), 1.0),
        "w_ada": nrm((DEPTH, 2, D, 3 * D), 0.2 * D ** -0.5),
        "b_ada": nrm((DEPTH, 2, 3 * D), 0.02),
        "ln_g": 1.0 + nrm((DEPTH, 2, D), 0.02),
        "ln_b": nrm((DEPTH, 2, D), 0.02),
        "w_in_even": nrm((N_EVEN, D, IN0_WIDTH), D ** -0.5),
        "w_a2": nrm((N_EVEN, GLA_GATE_RANK, GLA_KW), GLA_GATE_RANK ** -0.5),
        "b_a": nrm((N_EVEN, GLA_KW), 0.1),
        "gla_norm_g": 1.0 + nrm((N_EVEN, GLA_VW), 0.02),
        "conv_w": nrm((N_EVEN, CONV_WIDTH, CONV_CH), CONV_WIDTH ** -0.5),
        "conv_b": nrm((N_EVEN, CONV_CH), 0.02),
        "conv_ln_g": 1.0 + nrm((N_EVEN, CONV_CH), 0.02),
        "conv_ln_b": nrm((N_EVEN, CONV_CH), 0.02),
        "w_out_even": nrm((N_EVEN, MIX0_WIDTH, D), BETA * MIX0_WIDTH ** -0.5),
        "w_grp_pool": nrm((N_ODD, POOL_GROUPS, POOL_GC, POOL_GC), POOL_GC ** -0.5),
        "pool_scale": 1.0 + nrm((N_ODD, D), 0.1),
        "w_out_odd": nrm((N_ODD, D, D), BETA * D ** -0.5),
        "w_coarse": nrm((DEPTH, D, MOE_GROUPS), D ** -0.5),
        "b_coarse": nrm((DEPTH, MOE_GROUPS), 0.01),
        "w_fine": nrm((DEPTH, MOE_GROUPS, D, MOE_EXPERTS), D ** -0.5),
        "b_fine": nrm((DEPTH, MOE_GROUPS, MOE_EXPERTS), 0.01),
        "w_gate": nrm((DEPTH, MOE_GROUPS, MOE_EXPERTS, D, MOE_FF), D ** -0.5),
        "w_up": nrm((DEPTH, MOE_GROUPS, MOE_EXPERTS, D, MOE_FF), D ** -0.5),
        "w_down": nrm((DEPTH, MOE_GROUPS, MOE_EXPERTS, MOE_FF, D), BETA * MOE_FF ** -0.5),
    }

def reference(x_prompt, x_sample, state_gla, state_conv, state_pool, c_prompt, c_sample,
              w_ada, b_ada, ln_g, ln_b, w_in_even, w_a2, b_a, gla_norm_g, conv_w, conv_b,
              conv_ln_g, conv_ln_b, w_out_even, w_grp_pool, pool_scale, w_out_odd,
              w_coarse, b_coarse, w_fine, b_fine, w_gate, w_up, w_down):
    p = dict(w_ada=w_ada, b_ada=b_ada, ln_g=ln_g, ln_b=ln_b, w_in_even=w_in_even, w_a2=w_a2, b_a=b_a,
             gla_norm_g=gla_norm_g, conv_w=conv_w, conv_b=conv_b, conv_ln_g=conv_ln_g,
             conv_ln_b=conv_ln_b, w_out_even=w_out_even, w_grp_pool=w_grp_pool, pool_scale=pool_scale,
             w_out_odd=w_out_odd, w_coarse=w_coarse, b_coarse=b_coarse, w_fine=w_fine, b_fine=b_fine,
             w_gate=w_gate, w_up=w_up, w_down=w_down)
    z_gla = jnp.zeros((N_EVEN, BATCH) + state_gla.shape[2:], state_gla.dtype)
    z_conv = jnp.zeros((N_EVEN, BATCH) + state_conv.shape[2:], state_conv.dtype)
    z_pool = jnp.zeros((N_ODD, BATCH) + state_pool.shape[2:], state_pool.dtype)
    y_prompt, g_p, cv_p, pl_p = trunk(x_prompt, c_prompt, z_gla, z_conv, z_pool, 0, p)
    y_sample, g_s, cv_s, pl_s = trunk(x_sample, c_sample, state_gla, state_conv, state_pool, PAST_LEN, p)
    return (y_prompt, y_sample, g_p, cv_p, pl_p, g_s, cv_s, pl_s)


_drawn_inputs = setup_inputs


def setup_inputs(seed=0):
    import zlib

    import numpy as np

    out = dict(_drawn_inputs(seed))
    spreads = {}
    factors = {'gla_norm_g': 91.664,
     'conv_b': 7.001,
     'conv_ln_g': 82.606,
     'conv_ln_b': 84.382,
     'b_coarse': 8.0,
     'b_fine': 24.025}
    for name, (base, spread) in spreads.items():
        noise = np.random.default_rng([zlib.crc32(name.encode()), seed]).standard_normal(out[name].shape)
        drawn = base * np.exp(spread * noise) if base else spread * noise
        out[name] = __import__('jax').numpy.asarray(drawn.astype(out[name].dtype))
    for name, factor in factors.items():
        out[name] = (out[name] * factor).astype(out[name].dtype)
    return out
```

```python
from contextlib import ExitStack

import numpy as np

import concourse.bass as bass
from concourse import mybir

F32 = mybir.dt.float32
I32 = mybir.dt.int32
ALU = mybir.AluOpType
ACT = mybir.ActivationFunctionType
AX_X = mybir.AxisListType.X

P = 128
D = 1024
KD = D // P
SEQ = 256
NS = 8
T = SEQ + NS
TT = 3
HEADS, DK, DV = 4, 64, 128
TAPS = 31
HIST = TAPS - 1
CC = 4
PBUF = 15
WINDOWS = (2, 4, 8, 16)
EXPERTS = 16
FF = 512
KF = FF // P
C = 64
WIDE = 96
MAXCH = EXPERTS + (2 * T) // C + 1
ALPHA = (2 * 2) ** 0.25
EPS = 1e-5
TAU = 16.0
LEVELS = 7
NONE = 8192.0
FAR = 1e30
ADA_UNITS = 6

V_LNG, V_LNB, V_BA, V_GN, V_CB, V_CLG, V_CLB, V_PS, V_CW = 96, 128, 160, 162, 166, 170, 174, 178, 186
V_ALL = V_CW + TAPS * CC

K_ID, K_ONE, K_TRI = 0, 128, 256
K_MASK = 384
K_IOTA = K_MASK + 8 * 128
K_RCNT = K_IOTA + C
K_SELB = K_RCNT + 4 * SEQ
K_SELP = K_SELB + NS * C
K_SELC = K_SELP + 4 * NS
K_VALID = K_SELC + 2 * NS
K_DESC = K_VALID + TT
K_ALL = K_DESC + 4

U_ADA = [0, 11, 17, 25]
U_IN = 6
U_OE = 23
U_PRE = 31
RING = 6
U_OO = U_PRE + 3 * 16
MOE_BASE = [U_PRE, U_OO + 2]


def shape_constants():
    k = np.zeros((P, K_ALL), np.float32)
    i = np.arange(P)
    k[:, K_ID:K_ID + P] = np.eye(P)
    k[:, K_ONE:K_ONE + P] = 1.0
    k[:, K_TRI:K_TRI + P] = i[:, None] < i[None, :]
    k[:, K_MASK:K_MASK + P] = np.eye(P)
    for lv in range(LEVELS):
        b = 2 ** lv
        s, t = i[:, None] // b, i[None, :] // b
        k[:, K_MASK + P * (lv + 1):K_MASK + P * (lv + 2)] = (t == s + 1) & (s % 2 == 0)
    k[:, K_IOTA:K_IOTA + C] = np.arange(C)
    for w, win in enumerate(WINDOWS):
        k[:, K_RCNT + SEQ * w:K_RCNT + SEQ * (w + 1)] = 1.0 / np.minimum(win, np.arange(SEQ) + 1)
    for b in range(NS):
        k[b, K_SELB + C * b:K_SELB + C * (b + 1)] = 1.0
        for j in range(PBUF):
            for w, win in enumerate(WINDOWS):
                k[b * PBUF + j, K_SELP + NS * w + b] = float(j >= PBUF - (win - 1))
        for j in range(HIST):
            k[(b % 4) * HIST + j, K_SELC + NS * (b // 4) + b] = 1.0
    k[:, K_VALID:K_VALID + 2] = 1.0
    k[0:NS, K_VALID + 2] = 1.0
    k[:, K_DESC:K_DESC + 4] = np.arange(4, 0, -1)
    return k


class Steps:

    def __init__(self, eng, sem):
        self.eng, self.sem, self.value, self.done = eng, sem, {}, []

    def __call__(self, ins, signal=None):
        s = self.sem if signal is None else signal
        ins.then_inc(s, 1)
        self.value[s.name] = self.value.get(s.name, 0) + 1
        self.done.append((s, self.value[s.name]))
        return ins

    def sync(self, back=0):
        if len(self.done) > back:
            self.eng.wait_ge(*self.done[-1 - back])


def build(nc, I, O):
    with ExitStack() as ctx:
        def sb(name, shape, dt=F32):
            return ctx.enter_context(nc.sbuf_tensor(name, shape, dt))

        def sem(name):
            return ctx.enter_context(nc.semaphore(name))

        ring = sb("ring", [P, RING, 4096])
        con = sb("con", [P, K_ALL])
        vec = sb("vec", [P, V_ALL])
        x = sb("x", [P, KD, T])
        h = sb("h", [P, KD, T])
        t1 = sb("t1", [P, KD, T])
        t2 = sb("t2", [P, KD, T])
        acc = sb("acc", [P, KD, T])
        htm = sb("htm", [P, TT, D])
        stat = sb("stat", [P, T])
        ada = sb("ada", [P, 4, 24, 9])
        cT = sb("cT", [P, KD * 9 + WIDE - 9])
        wr = sb("wr", [P, 2, KD, 20])
        br = sb("br", [1, 2, 20])
        work = sb("work", [P, 9728])

        used = [0]

        def part(cols, restart=None):
            if restart is not None:
                used[0] = restart
            a = used[0]
            used[0] += cols
            assert used[0] <= 9728, used[0]
            return work[:, a:a + cols]

        q_ = part(2 * T, 0).rearrange("p (a t) -> p a t", t=T)
        k_ = part(2 * T).rearrange("p (a t) -> p a t", t=T)
        v_ = part(4 * T).rearrange("p (a t) -> p a t", t=T)
        g_ = part(4 * T).rearrange("p (a t) -> p a t", t=T)
        sg = part(4 * T).rearrange("p (a t) -> p a t", t=T)
        la = part(2 * T).rearrange("p (a t) -> p a t", t=T)
        la2 = part(2 * T).rearrange("p (a t) -> p a t", t=T)
        glu = part(CC * (HIST + T)).rearrange("p (a t) -> p a t", t=HIST + T)
        bcum = part(2 * SEQ)
        hf, t1f, t2f, af = (b[:, :, :].rearrange("p k t -> p (k t)") for b in (h, t1, t2, acc))
        dE = t1f[:, 0:4 * SEQ]
        qt = hf[:, 0:4 * SEQ].rearrange("p (a t) -> p a t", a=2)
        kt = hf[:, 4 * SEQ:8 * SEQ].rearrange("p (a t) -> p a t", a=2)
        att = t2f[:, 0:HEADS * 3 * P].rearrange("p (h b t) -> p h b t", h=HEADS, b=3)
        kltm = t2f[:, HEADS * (SEQ + P):HEADS * (SEQ + 2 * P)].rearrange("p (a n) -> p a n", a=4)
        vtm = af[:, 0:2 * FF].rearrange("p (a n) -> p a n", a=2)
        vstm = af[:, 2 * FF:3 * FF]
        cs = af[:, 0:2 * D].rearrange("p (a n) -> p a n", a=2)
        conv_prod = part(2 * FF).rearrange("p (a n) -> p a n", a=2)
        wrep = part(FF)
        alr = stat[:, :]
        asmp = part(2 * NS).rearrange("p (a t) -> p a t", a=2)
        gfin = part(2 * DV).rearrange("p (a n) -> p a n", a=2)
        conv_rows = part(FF)
        ysmp = part(CC * NS).rearrange("p (c b) -> p c b", c=CC)
        wa2 = part(SEQ)
        walr = part(KD * 16).rearrange("p (k n) -> p k n", k=KD)
        state = htm[:, 0:2, :].rearrange("p a (b n) -> p (a b) n", n=2 * DV)
        PW = 16 + SEQ
        pa = part(KD * PW, 0).rearrange("p (k t) -> p k t", k=KD)
        pb = part(KD * PW).rearrange("p (k t) -> p k t", k=KD)
        wgrp = part(4 * 2 * SEQ).rearrange("p (g c n) -> p g c n", g=4, c=2)
        pbuf = part(D)
        prow = part(D)
        psmp = part(KD * NS).rearrange("p (k b) -> p k b", k=KD)
        hg = part(KD * C, 0)
        hg_pad = part(WIDE - C)
        sel = part(TT * C)
        sel_pad = part(WIDE - C)
        selw = part(TT * C).rearrange("p (t n) -> p t n", t=TT)
        hot = [part(TT * C).rearrange("p (t n) -> p t n", t=TT) for _ in range(2)]
        sig = part(KF * C).rearrange("p (k n) -> p k n", k=KF)
        hid = part(KF * C)

        hg_x = work[:, 0:KD * C + WIDE - C]
        sel_x = work[:, KD * C + WIDE - C:(KD + TT) * C + 2 * (WIDE - C)]

        ytm = part(D)
        sct = part(T)
        lg = part(TT * 20).rearrange("p (t n) -> p t n", t=TT)
        mask = part(TT * EXPERTS).rearrange("p (t n) -> p t n", t=TT)
        pick = [part(TT * EXPERTS).rearrange("p (t n) -> p t n", t=TT) for _ in range(2)]
        cnt = part(EXPERTS)
        nch = part(EXPERTS)
        incl = part(EXPERTS)
        tabf = part(EXPERTS + 1)
        rank = part(TT * EXPERTS).rearrange("p (t n) -> p t n", t=TT)
        prod = part(TT * EXPERTS).rearrange("p (t n) -> p t n", t=TT)
        prod2 = part(TT * EXPERTS).rearrange("p (t n) -> p t n", t=TT)
        small = [part(TT * 4).rearrange("p (t n) -> p t n", t=TT) for _ in range(12)]
        one = [part(TT).rearrange("p (t n) -> p t n", n=1) for _ in range(8)]
        gslot = part(2 * TT)
        wsel = part(2 * TT)
        outb = htm
        tab = [sb(f"chunk_table{l}", [P, EXPERTS + 1], I32) for l in range(2)]
        onef = sb("onef", [P, EXPERTS])
        epsb = sb("epsb", [P, 1])
        rowsA = t2f[:, 0:3 * P].rearrange("p (a n) -> p a n", a=3)

        ident = con[:, K_ID:K_ID + P]
        ones = con[:, K_ONE:K_ONE + P]
        tri = con[:, K_TRI:K_TRI + P]
        iota = con[:, K_IOTA:K_IOTA + C]

        bank = [ctx.enter_context(nc.psum_tensor(f"bank{i}", [P, 512], F32)) for i in range(8)]
        ADA = bank[7]

        s_con, s_rows, s_x, s_c, s_small, s_state, s_hist = map(sem, (
            "constants_in", "vectors_in", "x_in", "c_in", "small_in", "state_in", "history_in"))
        s_mix1 = sem("mixer1_small_in")
        unit_in = [sem(f"slot_filled{i}") for i in range(RING)]
        s_out = sem("stored")
        act_n, dve_n, pool_n = sem("act_steps"), sem("dve_steps"), sem("pool_steps")
        ev = {}

        def E(name):
            if name not in ev:
                ev[name] = sem(name)
            return ev[name]

        def unit_free(eng, u):
            if u >= U_OO:
                eng.wait_ge(E("out1_done"), 4 * (u - U_OO + 1))
            elif u in (U_OE, U_OE + 1):
                eng.wait_ge(E("out0_done"), 4 * (u - U_OE + 1))
            elif U_IN <= u < U_IN + 5:
                eng.wait_ge(E("z_done"), Z_TILES.index((("qk", "ug", "ua", "v", "g")[u - U_IN], 3)) + 1)
            else:
                s = max(i for i in range(4) if U_ADA[i] <= u)
                eng.wait_ge(E("ada_units"), ADA_UNITS * s + u - U_ADA[s] + 1)

        def unit_ready(pe, u):
            pe.wait_ge(unit_in[u % RING], 16 * (u // RING + 1))

        def slot(u, m):
            return ring[:, u % RING, :].rearrange("p (k n) -> p k n", k=m)

        def bcast(ap, shape):
            return ap.broadcast_to(shape)

        w_in = I["w_in_even"][0]
        zcols = {"q": 0, "k": 256, "v": 512, "g": 1024, "alr": 1536, "ua": 1552, "ug": 2064}

        def ksplit(ap):
            return ap.rearrange("(k p) n -> p k n", p=P)

        stream = []
        for s in (0, ):
            stream += [ksplit(I["w_ada"][s // 2, s % 2][:, FF * n:FF * (n + 1)]) for n in range(ADA_UNITS)]
        stream += [ksplit(w_in[:, a:a + FF]) for a in (0, zcols["ug"], zcols["ua"], zcols["v"], zcols["g"])]
        for s in (1, 2):
            stream += [ksplit(I["w_ada"][s // 2, s % 2][:, FF * n:FF * (n + 1)]) for n in range(ADA_UNITS)]
        stream += [ksplit(I["w_out_even"][0][:, FF * n:FF * (n + 1)]) for n in range(2)]
        stream += [ksplit(I["w_ada"][1, 1][:, FF * n:FF * (n + 1)]) for n in range(ADA_UNITS)]
        assert len(stream) == U_PRE

        M = [{n: sem(f"{n}{l}") for n in (
            "table_ready", "hot_ready", "sel_ready", "hot_weighted", "selw_ready", "gather_done", "selwt_done",
            "gateup_done", "down_done", "scatter_products", "hg_copied", "sig_done", "t_done",
            "hid_done", "yt_copied_a", "yt_copied_d", "sct_copied", "scatter_adds", "zeroed",
            "slots_moved")} for l in range(2)]

        VEC_ROWS = []
        for col, t, r0, name in ((0, 0, 0, "b_ada"), (V_LNG, 1, 0, "ln_g"), (V_LNB, 1, 32, "ln_b"),
                                 (V_BA, 1, 64, "b_a"), (V_GN, 1, 66, "gla_norm_g"), (V_CB, 1, 70, "conv_b"),
                                 (V_CLG, 1, 74, "conv_ln_g"), (V_CLB, 1, 78, "conv_ln_b"),
                                 (V_PS, 1, 82, "pool_scale"), (V_CW, 2, 0, "conv_w")):
            a = I[name]
            lead = " ".join("abc"[:len(a.shape) - 1])
            VEC_ROWS.append((col, r0, t, a.rearrange(f"{lead} (n p) -> ({lead} n) p", p=P)))
        N_ROWS, N_SMALL, N_ROUTE, N_HIST = len(VEC_ROWS), 8, 14, 2

        Z_TILES = ([("alr", 0)] + [("qk", n) for n in range(4)] + [("la", n) for n in range(2)]
                   + [(nm, n) for nm in ("ug", "ua", "v", "g") for n in range(4)])
        Z_BY = ["d" if nm in ("la", "ua") else "a" for nm, _ in Z_TILES]
        Z_COUNT = {w: Z_BY.count(w) for w in "ad"}

        def z_free(eng, i):
            eng.wait_ge(E("z_copied_" + Z_BY[i]), Z_BY[:i + 1].count(Z_BY[i]))

        block = ctx.enter_context(nc.Block())

        @block.sync
        def _(sp):
            sp.dma_start(con[:, :], I["shape_constants"]).then_inc(s_con, 16)
            sp.dma_start(cs[0:1, 0, :], I["c_prompt"]).then_inc(s_c, 16)
            sp.dma_start(cs[1:9, 0, :], I["c_sample"]).then_inc(s_c, 16)
            sp.wait_ge(s_rows, 16 * N_ROWS)
            sp.wait_ge(s_x, 32)
            for u, src in enumerate(stream):
                if u >= RING:
                    unit_free(sp, u - RING)
                sp.dma_start(ring[:, u % RING, :].rearrange("p (k n) -> p k n", k=KD), src)\
                    .then_inc(unit_in[u % RING], 16)

            def expert_unit(l, i, e1):
                name = ("w_gate", "w_up", "w_down")[i]
                w = I[name][l].rearrange("g e d f -> (g e) d f")[e1]
                if not isinstance(e1, int):
                    w = w.rearrange("a d f -> (a d) f")
                return w.rearrange("(k p) n -> p k n", p=P)

            def fill_first_two(l, free):
                for n in range(RING):
                    free[n]()
                    u = MOE_BASE[l] + n
                    sp.dma_start(slot(u, KD if n % 3 < 2 else KF), expert_unit(l, n % 3, n // 3))\
                        .then_inc(unit_in[u % RING], 16)

            def fill_rest(l):
                sp.wait_ge(M[l]["table_ready"], 1)
                with sp.Fori(1, EXPERTS // 2) as ep:
                    for j in range(2):
                        e = sp.snap(2 * ep + j)
                        chunks = sp.value_load(tab[l][0:1, bass.ds(e - 1, 1)], min_val=1, max_val=MAXCH)
                        for i in range(3):
                            u = MOE_BASE[l] + 3 * j + i
                            sp.wait_ge(M[l]["gateup_done" if i < 2 else "down_done"], chunks)
                            sp.dma_start(slot(u, KD if i < 2 else KF), expert_unit(l, i, bass.ds(e, 1)))\
                                .then_inc(unit_in[u % RING], 16)

            fill_first_two(0, [lambda n=n: unit_free(sp, U_PRE + n - RING) for n in range(RING)])
            fill_rest(0)
            chunks14 = sp.value_load(tab[0][0:1, EXPERTS - 1:EXPERTS], min_val=1, max_val=MAXCH)
            chunks15 = sp.value_load(tab[0][0:1, EXPERTS:EXPERTS + 1], min_val=1, max_val=MAXCH)
            for n in range(2):
                u = U_OO + n
                sp.wait_ge(M[0]["gateup_done"], chunks14)
                sp.dma_start(slot(u, KD), ksplit(I["w_out_odd"][0][:, FF * n:FF * (n + 1)]))\
                    .then_inc(unit_in[u % RING], 16)
            fill_first_two(1, [lambda: sp.wait_ge(M[0]["down_done"], chunks14),
                               lambda: sp.wait_ge(M[0]["gateup_done"], chunks15),
                               lambda: sp.wait_ge(M[0]["gateup_done"], chunks15),
                               lambda: sp.wait_ge(M[0]["down_done"], chunks15),
                               lambda: unit_free(sp, U_OO),
                               lambda: unit_free(sp, U_OO + 1)])
            fill_rest(1)

        @block.tensor
        def _(pe):
            mm, tr = nc.tensor.matmul, nc.tensor.transpose

            def ada_unit(s, n):
                u = U_ADA[s] + n
                if n == 0:
                    pe.wait_ge(E("cT_ready"), 1)
                    if s:
                        pe.wait_ge(E("ada_copied"), s)
                unit_ready(pe, u)
                w = slot(u, KD)
                for m in range(4):
                    for k in range(KD):
                        c0 = 9 * (4 * n + m)
                        last = mm(ADA[:, c0:c0 + WIDE], w[:, k, P * m:P * (m + 1)], cT[:, 9 * k:9 * k + WIDE],
                                  start=(k == 0), stop=(k == KD - 1))
                last.then_inc(E("ada_units"), 1)

            def column_sums(name, src, dst):
                n = len(src)
                for i in range(n):
                    last = mm(dst, ones, src[i], start=(i == 0), stop=(i == n - 1))
                last.then_inc(E(name), 1)

            def layer_norm_sums(idx):
                pe.wait_ge(E("ln_r"), idx + 1)
                column_sums("ln_sum", [t1[:, k, :] for k in range(KD)], bank[0][:, 0:T])
                pe.wait_ge(E("ln_sq"), idx + 1)
                column_sums("ln_var", [t2[:, k, :] for k in range(KD)], bank[1][:, 0:T])

            def token_major(use, src):
                pe.wait_ge(E("tm_src"), use + 1)
                for t in range(TT):
                    n = min(P, T - t * P)
                    for hf in range(2):
                        b = bank[2 * t + hf]
                        for m in range(4):
                            last = tr(b[0:n, P * m:P * (m + 1)], src[:, 4 * hf + m, t * P:t * P + n], ident)
                        last.then_inc(E("tm_tr"), 1)

            def routing(l):
                for t in range(TT):
                    n = min(P, T - t * P)
                    o = bank[6][0:n, 20 * t:20 * t + 20]
                    for k in range(KD):
                        mm(o, h[:, k, t * P:t * P + n], wr[:, l, k, :], start=(k == 0), stop=False)
                    last = mm(o, ones[0:1, 0:n], br[0:1, l, :], start=False, stop=True)
                last.then_inc(E("route_logits"), 1)

            def ranks(l):
                pe.wait_ge(E("route_mask"), l + 1)
                for t in range(TT + 1):
                    o = bank[7][:, EXPERTS * t:EXPERTS * (t + 1)]
                    n = min(t + 1, TT)
                    for i in range(n):
                        last = mm(o, tri if i == t else ones, mask[:, i, :], start=(i == 0), stop=(i == n - 1))
                last.then_inc(E("route_ranks"), 1)

            def moe(l):
                m = M[l]
                G, GU, YT, ST, SC = bank[0], bank[1], (bank[3], bank[4]), bank[5], (bank[6], bank[7])

                def gather():
                    for f in range(KD):
                        n = min(WIDE, 512 - C * f)
                        for t in range(TT):
                            last = mm(G[:, C * f:C * f + n], htm[:, t, P * f:P * (f + 1)], sel_x[:, C * t:C * t + n],
                                      start=(t == 0), stop=(t == TT - 1))
                    last.then_inc(m["gather_done"], 1)

                def scatter_ready(g1):
                    pe.wait_ge(m["yt_copied_a"], g1)
                    pe.wait_ge(m["yt_copied_d"], g1)
                    pe.wait_ge(m["sct_copied"], g1)

                def scatter(f, adds):
                    pe.wait_ge(m["scatter_adds"], adds[f])
                    mm(SC[f % 2][:, 0:T], ytm[0:C, P * f:P * (f + 1)], sct[0:C, :],
                       start=True, stop=True).then_inc(m["scatter_products"], 1)

                def adds_before(g):
                    return [pe.snap((g + 1) * KD + max(f - 1, 0)) for f in range(KD)]

                pe.wait_ge(E("tm_a"), TT * (l + 1))
                pe.wait_ge(E("tm_d"), TT * (l + 1))
                pe.sem_inc(m["gather_done"], 1)
                pe.sem_inc(m["selwt_done"], 1)
                pe.wait_ge(m["zeroed"], 1)
                pe.wait_ge(m["table_ready"], 1)
                pe.wait_ge(m["sel_ready"], 1)
                gather()
                with pe.Fori(0, EXPERTS // 2) as ep:
                    for j in range(2):
                        u = MOE_BASE[l] + 3 * j
                        lo = pe.value_load(tab[l][0:1, bass.ds(2 * ep + j, 1)], min_val=0, max_val=MAXCH)
                        hi = pe.value_load(tab[l][0:1, bass.ds(2 * ep + j + 1, 1)], min_val=1, max_val=MAXCH)
                        filled = [pe.snap((ep + ((u + i) // RING + 1)) * 16) for i in range(3)]
                        wg, wu, wd = slot(u, KD), slot(u + 1, KD), slot(u + 2, KF)
                        with pe.Fori(lo, hi) as g:
                            g1 = pe.snap(g + 1)
                            g2 = pe.snap(g + 2)
                            adds = adds_before(g)
                            pe.wait_ge(m["hg_copied"], g1)
                            pe.wait_ge(m["hid_done"], g1)
                            for i, w in enumerate((wg, wu)):
                                pe.wait_ge(unit_in[(u + i) % RING], filled[i])
                                for f in range(KF):
                                    c0 = C * (KF * i + f)
                                    n = min(WIDE, 512 - c0)
                                    for k in range(KD):
                                        last = mm(GU[:, c0:c0 + n], w[:, k, P * f:P * (f + 1)],
                                                  hg_x[:, C * k:C * k + n],
                                                  start=(k == 0), stop=(k == KD - 1))
                            last.then_inc(m["gateup_done"], 1)
                            pe.wait_ge(m["sel_ready"], g2)
                            gather()
                            pe.wait_ge(m["selw_ready"], g1)
                            scatter_ready(g1)
                            for f in range(KD):
                                scatter(f, adds)
                                if f == 0:
                                    pe.wait_ge(m["hid_done"], g2)
                                    pe.wait_ge(unit_in[(u + 2) % RING], filled[2])
                                half, k = divmod(f, KF)
                                last = mm(YT[half][0:C, :], hid[:, C * k:C * (k + 1)],
                                          wd[:, k, 512 * half:512 * (half + 1)], start=(k == 0), stop=(k == KF - 1))
                            last.then_inc(m["down_done"], 1)
                            for t in range(TT):
                                n = min(P, T - t * P)
                                last = tr(ST[0:C, t * P:t * P + n], selw[0:n, t, :], ident[0:n, 0:n])
                            last.then_inc(m["selwt_done"], 1)
                total = pe.value_load(tab[l][0:1, EXPERTS:EXPERTS + 1], min_val=EXPERTS, max_val=MAXCH)
                end = pe.snap(total + 1)
                adds = adds_before(total)
                pe.wait_ge(m["hg_copied"], end)
                scatter_ready(end)
                for f in range(KD):
                    scatter(f, adds)

            pe.wait_ge(s_con, 16)
            pe.wait_ge(s_rows, 16 * N_ROWS)
            for i, n in enumerate((96, 90, 124)):
                o = (0, 96, 186)[i]
                last = tr(bank[6][:, o:o + n], rowsA[0:n, i, :], ident[0:n, 0:n])
            last.then_inc(E("vec_tr"), 1)
            pe.wait_ge(E("silu_c"), 1)
            for k in range(KD):
                last = tr(bank[5][:, 9 * k:9 * k + 9], cs[0:9, 0, P * k:P * (k + 1)], ident[0:9, 0:9])
            last.then_inc(E("c_tr"), 1)
            pe.wait_ge(s_x, 32)
            for k in range(KD):
                if k >= 4:
                    pe.wait_ge(E("x_copied"), k - 3)
                for t in range(TT):
                    n = min(P, T - t * P)
                    last = tr(bank[k % 4][:, t * P:t * P + n], htm[0:n, t, P * k:P * (k + 1)], ident[0:n, 0:n])
                last.then_inc(E("x_tr"), 1)
            for n in range(ADA_UNITS):
                ada_unit(0, n)

            pe.wait_ge(E("h0_ready"), 1)
            for i, (name, n) in enumerate(Z_TILES):
                o = bank[i % 6]
                if i >= 6:
                    z_free(pe, i - 6)
                else:
                    pe.wait_ge(E("x_copied"), KD)
                    pe.wait_ge(E("cT_ready"), 1)
                if name == "alr":
                    pe.wait_ge(s_small, 16 * N_SMALL)
                    for k in range(KD):
                        last = mm(o[0:16, 0:T], walr[:, k, :], h[:, k, :], start=(k == 0), stop=(k == KD - 1))
                elif name == "la":
                    z_free(pe, 0)
                    last = mm(o[:, 0:T], wa2[0:16, P * n:P * (n + 1)], alr[0:16, :], start=True, stop=True)
                else:
                    u = U_IN + ("qk", "ug", "ua", "v", "g").index(name)
                    if n == 0:
                        unit_ready(pe, u)
                    w = slot(u, KD)
                    for k in range(KD):
                        last = mm(o[:, 0:T], w[:, k, P * n:P * (n + 1)], h[:, k, :],
                                  start=(k == 0), stop=(k == KD - 1))
                last.then_inc(E("z_done"), 1)

            for n in range(ADA_UNITS):
                ada_unit(1, n)
            z_free(pe, len(Z_TILES) - 1)
            pe.wait_ge(E("z_copied_a"), Z_COUNT["a"])
            pe.wait_ge(E("z_copied_d"), Z_COUNT["d"])
            for tt in range(2):
                for hd in range(HEADS):
                    last = tr(bank[4 + tt][:, P * hd:P * (hd + 1)], v_[:, hd, P * tt:P * (tt + 1)], ident)
                last.then_inc(E("v_tr"), 1)
            for s in range(LEVELS + 2):
                pe.wait_ge(E("level_qk"), s + 1)
                if s >= 2:
                    pe.wait_ge(E("level_copied"), s - 1)
                qs, ks = (q_, k_) if s == 0 else (qt[:, :, SEQ * (s % 2):SEQ * (s % 2 + 1)],
                                                 kt[:, :, SEQ * (s % 2):SEQ * (s % 2 + 1)])
                n = 2 if s <= LEVELS else 1
                for hd in range(HEADS):
                    o, r = bank[2 * (s % 2) + hd % 2], slice(DK * (hd % 2), DK * (hd % 2 + 1))
                    for tt in range(n):
                        tq = tt if s <= LEVELS else 1
                        c0 = P * (n * (hd // 2) + tt)
                        last = mm(o[:, c0:c0 + P], ks[r, hd // 2, P * tt:P * (tt + 1)],
                                  qs[r, hd // 2, P * tq:P * (tq + 1)], start=True, stop=True)
                last.then_inc(E("level_done"), 1)
                if s < ADA_UNITS:
                    ada_unit(2, s)
            pe.wait_ge(E("level_copied"), LEVELS + 2)
            pe.wait_ge(E("vtm_copied"), 2)
            for hd in range(HEADS):
                o = bank[hd // 2][:, SEQ * (hd % 2):SEQ * (hd % 2 + 1)]
                mm(o.rearrange("p (b t) -> p b t", b=2), vtm[:, 0, P * hd:P * (hd + 1)], att[:, hd, 0:3:2, :],
                   start=True, stop=False)
                last = mm(o[:, P:SEQ], vtm[:, 1, P * hd:P * (hd + 1)], att[:, hd, 1, :], start=False, stop=True)
            last.then_inc(E("o_done"), 1)
            pe.wait_ge(E("kl_ready"), 1)
            for a in range(2):
                for tt in range(2):
                    last = tr(bank[4][:, P * (2 * a + tt):P * (2 * a + tt + 1)],
                              kt[:, a, P * tt:P * (tt + 1)], ident)
            last.then_inc(E("kl_tr"), 1)
            for hd in range(HEADS):
                last = tr(bank[5][0:NS, P * hd:P * (hd + 1)], v_[:, hd, SEQ:T], ident)
            last.then_inc(E("vs_tr"), 1)
            pe.wait_ge(E("kl_copied"), 1)
            for hd in range(HEADS):
                r = slice(DK * (hd % 2), DK * (hd % 2 + 1))
                for tt in range(2):
                    last = mm(bank[6][r, DV * (hd // 2):DV * (hd // 2 + 1)], kltm[:, 2 * (hd // 2) + tt, r],
                              vtm[:, tt, P * hd:P * (hd + 1)], start=(tt == 0), stop=(tt == 1))
            last.then_inc(E("gfin_done"), 1)
            pe.wait_ge(E("o_copied"), 2)
            pe.wait_ge(E("vs_copied"), 1)
            vs4 = vstm[0:NS, :].rearrange("p (a two n) -> p two a n", two=2, n=DV)
            for i in range(4):
                for bb in range(2):
                    b = 2 * i + bb
                    for r in range(2):
                        last = mm(bank[i][DK * r:DK * (r + 1), SEQ * bb:SEQ * (bb + 1)].rearrange(
                                      "p (a n) -> p a n", a=2),
                                  con[0:NS, K_SELB + C * b:K_SELB + C * (b + 1)], vs4[:, r], start=True, stop=True)
                last.then_inc(E("vb_done"), 1)
            pe.wait_ge(E("state_new"), 1)
            for hd in range(HEADS):
                r = slice(DK * (hd % 2), DK * (hd % 2 + 1))
                for b in range(NS):
                    c0 = NS * (hd // 2) + b
                    last = mm(bank[4 + hd % 2][:, c0:c0 + 1],
                              state[r, b, DV * (hd // 2):DV * (hd // 2 + 1)],
                              q_[r, hd // 2, SEQ + b:SEQ + b + 1], start=True, stop=True)
            last.then_inc(E("os_done"), 1)
            pe.wait_ge(E("os_copied"), 2)
            pe.wait_ge(E("hist_prod"), 1)
            pe.wait_ge(E("gfin_copied"), 1)
            for c in range(CC):
                for i in range(2):
                    last = mm(bank[6][:, NS * c:NS * (c + 1)], conv_prod[0:4 * HIST, i, P * c:P * (c + 1)],
                              con[0:4 * HIST, K_SELC + NS * i:K_SELC + NS * (i + 1)], start=(i == 0), stop=(i == 1))
            last.then_inc(E("hist_done"), 1)
            for c in range(CC):
                last = tr(bank[5][0:HIST + NS, P * c:P * (c + 1)], glu[:, c, SEQ:HIST + T], ident)
            last.then_inc(E("conv_rows_tr"), 1)
            o_flat = t1[:, 0:4, :].rearrange("p a t -> p (a t)")
            sq_flat = t2[:, 0:4, :].rearrange("p a t -> p (a t)")
            OW = 4 * T // 3
            for i in range(3):
                last = mm(bank[i][:, 0:OW], ones, o_flat[:, OW * i:OW * (i + 1)], start=True, stop=True)
            last.then_inc(E("on_sum"), 1)
            pe.wait_ge(E("on_sq"), 1)
            for i in range(3):
                last = mm(bank[i][:, 0:OW], ones, sq_flat[:, OW * i:OW * (i + 1)], start=True, stop=True)
            last.then_inc(E("on_var"), 1)
            pe.wait_ge(E("cn_r"), 1)
            column_sums("cn_sum", [t1[:, 4 + c, :] for c in range(CC)], bank[3][:, 0:T])
            pe.wait_ge(E("cn_sq"), 1)
            column_sums("cn_var", [t2[:, 4 + c, :] for c in range(CC)], bank[4][:, 0:T])

            def projection(name, u, src):
                for m in range(KD):
                    if m >= 4:
                        pe.wait_ge(E(name + "_taken"), m - 3)
                    if m % 4 == 0:
                        unit_ready(pe, u + m // 4)
                    w = slot(u + m // 4, KD)
                    for k in range(KD):
                        last = mm(bank[m % 4][:, 0:T], w[:, k, P * (m % 4):P * (m % 4 + 1)], src[:, k, :],
                                  start=(k == 0), stop=(k == KD - 1))
                    last.then_inc(E(name + "_done"), 1)

            pe.wait_ge(E("out0_src"), 1)
            projection("out0", U_OE, acc)
            for n in range(3):
                ada_unit(3, n)
            pe.wait_ge(E("ln_r"), 1)
            layer_norm_sums(0)
            for n in range(3, ADA_UNITS):
                ada_unit(3, n)
            pe.wait_ge(s_mix1, 16 * N_ROUTE)
            pe.wait_ge(E("tm_src"), 1)
            routing(0)
            token_major(0, h)
            pe.wait_ge(E("ada_copied"), 4)
            ranks(0)
            pe.wait_ge(E("rank_copied"), 1)
            moe(0)
            layer_norm_sums(1)
            pe.wait_ge(s_hist, 16 * N_HIST)
            pe.wait_ge(E("pool_src"), 1)
            for k in range(KD):
                last = tr(bank[4 + k // 4][0:PBUF + NS, P * (k % 4):P * (k % 4 + 1)], h[:, k, SEQ - PBUF:T], ident)
            last.then_inc(E("pool_rows_tr"), 1)
            for k in range(KD):
                last = mm(bank[6][:, NS * k:NS * (k + 1)], pbuf[0:NS * PBUF, P * k:P * (k + 1)],
                          con[0:NS * PBUF, K_SELP + NS * (k // 2):K_SELP + NS * (k // 2 + 1)], start=True, stop=True)
            last.then_inc(E("pool_hist_done"), 1)
            pe.wait_ge(E("pooled"), 1)
            for m in range(KD):
                g, hf = m // 2, m % 2
                if m >= 4:
                    pe.wait_ge(E("grp_copied"), m - 3)
                for c in range(2):
                    last = mm(bank[m % 4][:, 0:T], wgrp[:, g, c, P * hf:P * (hf + 1)], t1[:, 2 * g + c, :],
                              start=(c == 0), stop=(c == 1))
                last.then_inc(E("grp_done"), 1)
            pe.wait_ge(E("grp_copied"), KD)
            projection("out1", U_OO, t2)
            layer_norm_sums(2)
            pe.wait_ge(E("tm_src"), 2)
            routing(1)
            token_major(1, h)
            ranks(1)
            pe.wait_ge(E("rank_copied"), 2)
            moe(1)
            layer_norm_sums(3)
            token_major(2, x)

        @block.scalar
        def _(act):
            fn = nc.scalar.activation
            A = Steps(act, act_n)

            def copy(dst, src, signal=None, scale=1.0):
                return A(fn(dst, src, ACT.Copy, scale=scale), signal)

            for _, r, c, src in VEC_ROWS:
                act.dma_start(rowsA[r:r + src.shape[0], c, :], src).then_inc(s_rows, 16)
            act.dma_start(htm[:, 0:2, :], I["x_prompt"][0].rearrange("(t p) d -> p t d", p=P)).then_inc(s_x, 16)
            act.wait_ge(E("htm_zeroed"), 1)
            act.dma_start(htm[0:NS, 2, :], I["x_sample"][:, 0, :]).then_inc(s_x, 16)

            act.wait_ge(s_c, 32)
            A(fn(cs[0:9, 1, :], cs[0:9, 0, :], ACT.Sigmoid), E("c_sig"))
            for k in range(KD):
                act.wait_ge(E("x_tr"), k + 1)
                copy(x[:, k, :], bank[k % 4][:, 0:T], E("x_copied"))

            for i, (name, n) in enumerate(Z_TILES):
                if name == "v" and n == 0:
                    act.wait_ge(E("la_abs"), 1)
                    A(fn(la2, la2, ACT.Exp, scale=-1.0))
                    A.sync()
                    A(fn(la2, la2, ACT.Ln, bias=onef[:, 0:1]), E("la_ln"))
                if Z_BY[i] != "a":
                    continue
                act.wait_ge(E("z_done"), i + 1)
                b = bank[i % 6]
                if name == "alr":
                    copy(alr[0:16, :], b[0:16, 0:T], E("z_copied_a"))
                elif name == "qk" and n < 2:
                    copy(q_[:, n, :], b[:, 0:T], E("z_copied_a"), scale=DK ** -0.5)
                elif name == "qk":
                    copy(k_[:, n - 2, :], b[:, 0:T], E("z_copied_a"))
                elif name == "ug":
                    A(fn(sg[:, n, :], b[:, 0:T], ACT.Sigmoid), E("z_copied_a"))
                elif name == "v":
                    copy(v_[:, n, :], b[:, 0:T], E("z_copied_a"))
                else:
                    z_free(act, Z_TILES.index(("ua", n)))
                    A(fn(sg[:, n, :], b[:, 0:T], ACT.Sigmoid))
                    copy(g_[:, n, :], b[:, 0:T], E("z_copied_a"))

            act.wait_ge(E("la_done"), 1)
            A(fn(asmp, la[:, :, SEQ:T], ACT.Exp), E("a_exp"))
            for tt in range(2):
                act.wait_ge(E("v_tr"), tt + 1)
                copy(vtm[:, tt, :], bank[4 + tt][:, :], E("vtm_copied"))
            for s in range(1, LEVELS + 2):
                act.wait_ge(E("level_diff"), s)
                A(fn(dE[:, 2 * SEQ * (s % 2):2 * SEQ * (s % 2 + 1)], dE[:, 2 * SEQ * (s % 2):2 * SEQ * (s % 2 + 1)],
                     ACT.Exp), E("level_exp"))
            act.wait_ge(E("kl_diff"), 1)
            A(fn(dE[:, 0:2 * SEQ], dE[:, 0:2 * SEQ], ACT.Exp), E("kl_exp"))
            act.wait_ge(E("kl_ready"), 1)
            act.wait_ge(E("o_done"), 1)
            for i in range(2):
                copy(t1[:, 2 * i:2 * i + 2, 0:SEQ], bank[i][:, :].rearrange("p (a t) -> p a t", a=2), E("o_copied"))
            act.wait_ge(E("kl_tr"), 1)
            copy(kltm, bank[4][:, :].rearrange("p (a n) -> p a n", a=4), E("kl_copied"))
            act.wait_ge(E("vs_tr"), 1)
            copy(vstm[0:NS, :], bank[5][0:NS, :], E("vs_copied"))
            act.wait_ge(E("gfin_done"), 1)
            copy(gfin, bank[6][:, 0:2 * DV].rearrange("p (a n) -> p a n", a=2), E("gfin_copied"))
            act.wait_ge(E("os_done"), 1)
            for r in range(2):
                copy(t1[:, r:4:2, SEQ:T], bank[4 + r][:, 0:2 * NS].rearrange("p (a t) -> p a t", a=2), E("os_copied"))
            act.wait_ge(E("conv_rows_tr"), 1)
            copy(conv_rows[0:HIST + NS, :], bank[5][0:HIST + NS, :], E("conv_rows_copied"))
            act.wait_ge(E("on_c"), 1)
            A(fn(t2[:, 0:4, :], t1[:, 0:4, :], ACT.Square), E("on_sq"))
            act.wait_ge(E("cn_c"), 1)
            A(fn(t2[:, 4:8, :], t1[:, 4:8, :], ACT.Square), E("cn_sq"))
            act.wait_ge(E("on_var"), 1)
            sq_flat = t2[:, 0:4, :].rearrange("p a t -> p (a t)")
            OW = 4 * T // 3
            for i in range(3):
                A(fn(sq_flat[:, OW * i:OW * (i + 1)], bank[i][:, 0:OW], ACT.Sqrt, scale=1.0 / DV, bias=epsb[:, 0:1]),
                  E("on_std"))
            act.wait_ge(E("cn_var"), 1)
            A(fn(stat[:, :], bank[4][:, 0:T], ACT.Sqrt, scale=1.0 / FF, bias=epsb[:, 0:1]), E("cn_std"))
            act.wait_ge(E("cn_hat"), 1)
            for c in range(CC):
                A(fn(t2[:, 4 + c, :], t1[:, 4 + c, :], ACT.Sigmoid, scale=vec[:, V_CLG + c:V_CLG + c + 1],
                     bias=vec[:, V_CLB + c:V_CLB + c + 1]), E("cn_sig"))

            def layer_norm(idx):
                act.wait_ge(E("ln_c"), idx + 1)
                A(fn(t2[:, :, :], t1[:, :, :], ACT.Square), E("ln_sq"))
                act.wait_ge(E("ln_var"), idx + 1)
                A(fn(stat[:, :], bank[1][:, 0:T], ACT.Sqrt, scale=1.0 / D, bias=epsb[:, 0:1]), E("ln_std"))

            def token_major(use, dst):
                for t in range(TT):
                    n = min(P, T - t * P)
                    act.wait_ge(E("tm_tr"), 6 * use + 2 * t + 1)
                    copy(dst[0:n, t, 0:512], bank[2 * t][0:n, :], E("tm_a"))

            def routing(l):
                act.wait_ge(E("route_logits"), l + 1)
                act.wait_ge(E("logits_zeroed"), l + 1)
                for t in range(TT):
                    n = min(P, T - t * P)
                    copy(lg[0:n, t, :], bank[6][0:n, 20 * t:20 * t + 20])
                A.sync()
                copy(cnt[:, 0:1], con[:, 0:1], E("route_lg"))
                act.wait_ge(E("route_d1"), l + 1)
                A(fn(small[1], small[0], ACT.Exp), E("route_e1"))
                act.wait_ge(E("route_d2"), l + 1)
                A(fn(small[6], small[5], ACT.Exp), E("route_e2"))

            def moe(l):
                m = M[l]
                G, GU, YT = bank[0], bank[1], bank[3]
                flat = lambda ap: ap.rearrange("p k n -> p (k n)")
                act.wait_ge(m["table_ready"], 1)
                total = act.value_load(tab[l][0:1, EXPERTS:EXPERTS + 1], min_val=EXPERTS, max_val=MAXCH)
                act.sem_inc(m["yt_copied_a"], 1)
                act.wait_ge(m["gather_done"], 2)
                fn(hg, G[:, :], ACT.Copy).then_inc(m["hg_copied"], 1)
                with act.Fori(0, total) as g:
                    g1, g3 = act.snap(g + 1), act.snap(g + 3)
                    act.wait_ge(m["gateup_done"], g1)
                    fn(flat(sig), GU[:, 0:KF * C], ACT.Sigmoid).then_inc(m["sig_done"], 1)
                    act.wait_ge(m["gather_done"], g3)
                    fn(hg, G[:, :], ACT.Copy).then_inc(m["hg_copied"], 1)
                    act.wait_ge(m["down_done"], g1)
                    fn(ytm[0:C, 0:512], YT[0:C, :], ACT.Copy).then_inc(m["yt_copied_a"], 1)

            layer_norm(0)
            act.wait_ge(E("mix0_stored"), 1)
            routing(0)
            token_major(0, htm)
            moe(0)
            layer_norm(1)
            act.wait_ge(E("pool_rows_tr"), 1)
            for i in range(2):
                copy(prow[0:PBUF + NS, 512 * i:512 * (i + 1)], bank[4 + i][0:PBUF + NS, :], E("prow_copied"))
            for m in range(KD):
                act.wait_ge(E("grp_done"), m + 1)
                A(fn(t2[:, m, :], bank[m % 4][:, 0:T], ACT.Identity, scale=vec[:, V_PS + m:V_PS + m + 1]),
                  E("grp_copied"))
            layer_norm(2)
            routing(1)
            token_major(1, htm)
            moe(1)
            layer_norm(3)
            token_major(2, outb)

        @block.vector
        def _(dve):
            v = nc.vector
            S = Steps(dve, dve_n)

            def tt(out, a, b, op, signal=None):
                return S(v.tensor_tensor(out, a, b, op), signal)

            def ts(out, a, s1, s2, op0, op1, signal=None):
                return S(v.tensor_scalar(out, a, s1, s2, op0, op1), signal)

            def stt(out, a, s, b, op0, op1, signal=None):
                return S(v.scalar_tensor_tensor(out=out, in0=a, scalar=s, in1=b, op0=op0, op1=op1), signal)

            def one_op(out, a, s1, op, signal=None):
                return S(v.tensor_scalar(out, a, s1, None, op), signal)

            S(v.memset(htm[:, 2, :], 0.0), E("htm_zeroed"))
            S(v.memset(onef[:, :], 1.0))
            S(v.memset(epsb[:, :], EPS), E("small_consts"))
            S(v.memset(glu[:, :, 0:HIST], 0.0))
            dve.wait_ge(E("vec_tr"), 1)
            S(v.tensor_copy(vec[:, :], bank[6][:, 0:V_ALL]))
            dve.wait_ge(s_c, 32)
            dve.wait_ge(E("c_sig"), 1)
            tt(cs[0:9, 0, :], cs[0:9, 0, :], cs[0:9, 1, :], ALU.mult, E("silu_c"))
            dve.wait_ge(E("c_tr"), 1)
            S(v.memset(cT[:, 9 * KD:], 0.0))
            S(v.tensor_copy(cT[:, 0:9 * KD], bank[5][:, 0:9 * KD]), E("cT_ready"))

            def ada_copy(s):
                dve.wait_ge(E("ada_units"), ADA_UNITS * (s + 1))
                S.sync()
                tt(ada[:, s], ADA[:, 0:216].rearrange("p (m n) -> p m n", n=9),
                   vec[:, 24 * s:24 * (s + 1)].unsqueeze(2).broadcast_to([P, 24, 9]), ALU.add, E("ada_copied"))
                S.sync()
                one_op(ada[:, s, KD:3 * KD], ada[:, s, KD:3 * KD], 1.0, ALU.add)

            def modulate(s, signal=None):
                S.sync()
                for k in range(KD):
                    ts(h[:, k, 0:SEQ], x[:, k, 0:SEQ], ada[:, s, KD + k, 0:1], ada[:, s, k, 0:1], ALU.mult, ALU.add)
                tt(h[:, :, SEQ:T], x[:, :, SEQ:T], ada[:, s, KD:2 * KD, 1:9], ALU.mult)
                S.sync()
                tt(h[:, :, SEQ:T], h[:, :, SEQ:T], ada[:, s, 0:KD, 1:9], ALU.add, signal)
                one_op(x[:, :, :], x[:, :, :], ALPHA, ALU.mult)

            def residual(s, m, src, signal=None):
                stt(t1[:, m, 0:SEQ], src[:, 0:SEQ], ada[:, s, 2 * KD + m, 0:1], x[:, m, 0:SEQ], ALU.mult, ALU.add)
                tt(stat[:, NS * m:NS * (m + 1)], src[:, SEQ:T], ada[:, s, 2 * KD + m, 1:9], ALU.mult, signal)

            def residual_samples(signal=None):
                S.sync()
                tt(t1[:, :, SEQ:T], stat[:, 0:NS * KD].rearrange("p (k b) -> p k b", k=KD), x[:, :, SEQ:T],
                   ALU.add, signal)

            def layer_norm(idx):
                dve.wait_ge(E("ln_sum"), idx + 1)
                stt(t1[:, :, :], bank[0][:, 0:T].unsqueeze(1).broadcast_to([P, KD, T]), -1.0 / D, t1[:, :, :],
                    ALU.mult, ALU.add, E("ln_c"))
                dve.wait_ge(E("ln_std"), idx + 1)
                S(v.reciprocal(stat[:, :], stat[:, :]))
                S.sync()
                tt(t1[:, :, :], t1[:, :, :], stat[:, :].unsqueeze(1).broadcast_to([P, KD, T]), ALU.mult)
                S.sync()
                for k in range(KD):
                    ts(x[:, k, :], t1[:, k, :], vec[:, V_LNG + KD * idx + k:V_LNG + KD * idx + k + 1],
                       vec[:, V_LNB + KD * idx + k:V_LNB + KD * idx + k + 1], ALU.mult, ALU.add)

            ada_copy(0)
            dve.wait_ge(E("x_copied"), KD)
            modulate(0, E("h0_ready"))

            for i, (name, n) in enumerate(Z_TILES):
                if Z_BY[i] != "d":
                    continue
                dve.wait_ge(E("z_done"), i + 1)
                if name == "la":
                    one_op(la[:, n, :], bank[i % 6][:, 0:T], vec[:, V_BA + n:V_BA + n + 1], ALU.add, E("z_copied_d"))
                    if n == 1:
                        S.sync()
                        one_op(la2, la, -1.0, ALU.mult)
                        S.sync()
                        tt(la2, la2, la, ALU.max, E("la_abs"))
                else:
                    dve.wait_ge(E("z_copied_a"), Z_BY[:Z_TILES.index(("ug", n)) + 1].count("a"))
                    tt(glu[:, n, HIST:HIST + T], bank[i % 6][:, 0:T], sg[:, n, :], ALU.mult, E("z_copied_d"))
            dve.wait_ge(E("la_ln"), 1)
            stt(la, la, 0.0, la2, ALU.min, ALU.subtract)
            S.sync()
            one_op(la, la, 1.0 / TAU, ALU.mult, E("la_done"))
            S.sync()
            for a in range(2):
                S(v.tensor_tensor_scan(bcum[:, SEQ * a:SEQ * (a + 1)], con[:, K_ONE:K_ONE + 1].broadcast_to([P, SEQ]),
                                       la[:, a, 0:SEQ], 0.0, ALU.mult, ALU.add))

            def tap(j, c):
                return vec[:, V_CW + j * CC + c:V_CW + j * CC + c + 1]

            S.sync()
            for c in range(CC):
                ts(t1[:, 4 + c, 0:SEQ], glu[:, c, 0:SEQ], tap(0, c), vec[:, V_CB + c:V_CB + c + 1], ALU.mult, ALU.add)
            for j in range(1, TAPS):
                for c in range(CC):
                    S.sync(CC - 1)
                    stt(t1[:, 4 + c, 0:SEQ], glu[:, c, j:j + SEQ], tap(j, c), t1[:, 4 + c, 0:SEQ], ALU.mult, ALU.add)
            dve.wait_ge(s_small, 16 * N_SMALL)
            for i in range(2):
                tt(conv_prod[0:4 * HIST, i, :], conv_prod[0:4 * HIST, i, :], wrep[0:4 * HIST, :], ALU.mult,
                   E("hist_prod") if i else None)
            lastw = vec[:, V_CW + HIST * CC:V_CW + HIST * CC + CC].unsqueeze(2).broadcast_to([P, CC, NS])
            tt(ysmp, glu[:, :, HIST + SEQ:HIST + T], lastw, ALU.mult)
            S.sync()
            tt(ysmp, ysmp, vec[:, V_CB:V_CB + CC].unsqueeze(2).broadcast_to([P, CC, NS]), ALU.add)

            dve.wait_ge(E("z_copied_a"), Z_COUNT["a"])
            S(v.memset(epsb[:, :], EPS), E("level_qk"))

            def level_diff(s):
                b2 = 2 ** (s - 1)
                if s >= 3:
                    S.sync()
                view = lambda ap: ap.rearrange("p (m s j) -> p m s j", s=2, j=b2)
                bb, dd = view(bcum), view(dE[:, 2 * SEQ * (s % 2):2 * SEQ * (s % 2 + 1)])
                m = SEQ // b2
                ref = bb[:, :, 0, b2 - 1:b2].broadcast_to([P, m, b2])
                tt(dd[:, :, 1, :], bb[:, :, 1, :], ref, ALU.subtract)
                tt(dd[:, :, 0, :], ref, bb[:, :, 0, :], ALU.subtract, E("level_diff"))

            def level_qk(s):
                dve.wait_ge(E("level_exp"), s)
                if s >= 3:
                    dve.wait_ge(E("level_done"), s - 1)
                ex = dE[:, 2 * SEQ * (s % 2):2 * SEQ * (s % 2 + 1)].rearrange("p (a t) -> p a t", a=2)
                c = slice(SEQ * (s % 2), SEQ * (s % 2 + 1))
                tt(qt[:, :, c], q_[:, :, 0:SEQ], ex, ALU.mult)
                tt(kt[:, :, c], k_[:, :, 0:SEQ], ex, ALU.mult, E("level_qk"))

            def level_copy(s):
                dve.wait_ge(E("level_done"), s + 1)
                S.sync()
                for r in range(2):
                    sig = E("level_copied") if r else None
                    if s == LEVELS + 1:
                        S(v.tensor_copy(att[:, r:4:2, 2, :], bank[r][:, 0:2 * P].rearrange("p (a t) -> p a t", a=2)),
                          sig)
                        continue
                    o = bank[2 * (s % 2) + r][:, :].rearrange("p (a b t) -> p a b t", a=2, b=2)
                    mk = con[:, K_MASK + P * s:K_MASK + P * (s + 1)].unsqueeze(1).unsqueeze(1)\
                        .broadcast_to([P, 2, 2, P])
                    if s == 0:
                        tt(att[:, r:4:2, 0:2, :], o, mk, ALU.mult, sig)
                    else:
                        S(v.copy_predicated(att[:, r:4:2, 0:2, :], mk.bitcast(I32), o), sig)

            ada_copy(1)
            level_diff(1)
            for s in range(1, LEVELS + 2):
                if s <= LEVELS:
                    level_diff(s + 1)
                level_qk(s)
                level_copy(s - 1)
            level_copy(LEVELS + 1)
            S.sync()
            b3 = bcum.rearrange("p (a t) -> p a t", a=2)
            tt(dE[:, 0:2 * SEQ].rearrange("p (a t) -> p a t", a=2), b3[:, :, SEQ - 1:SEQ].broadcast_to([P, 2, SEQ]),
               b3, ALU.subtract, E("kl_diff"))
            dve.wait_ge(E("kl_exp"), 1)
            tt(kt[:, :, 0:SEQ], k_[:, :, 0:SEQ], dE[:, 0:2 * SEQ].rearrange("p (a t) -> p a t", a=2), ALU.mult,
               E("kl_ready"))

            dve.wait_ge(s_state, 32)
            dve.wait_ge(E("a_exp"), 1)
            st4 = state.rearrange("p b (a n) -> p b a n", a=2)
            for a in range(2):
                tt(st4[:, :, a, :], st4[:, :, a, :], asmp[:, a, :].unsqueeze(2).broadcast_to([P, NS, DV]), ALU.mult)
            S.sync()
            for i in range(4):
                dve.wait_ge(E("vb_done"), i + 1)
                for a in range(2):
                    pv = bank[i][:, :].rearrange("p (b a n) -> p b a n", b=2, a=2)[:, :, a, :]
                    tt(pv, pv, k_[:, a, SEQ + 2 * i:SEQ + 2 * i + 2].unsqueeze(2).broadcast_to([P, 2, DV]), ALU.mult)
                S.sync()
                tt(state[:, 2 * i:2 * i + 2, :], state[:, 2 * i:2 * i + 2, :],
                   bank[i][:, :].rearrange("p (b n) -> p b n", b=2), ALU.add, E("state_new") if i == 3 else None)

            OW = 4 * T // 3
            flat = t1[:, 0:4, :].rearrange("p a t -> p (a t)")
            for c in range(CC):
                one_op(g_[:, c, :], g_[:, c, :], vec[:, V_GN + c:V_GN + c + 1], ALU.mult)
            S.sync()
            tt(g_, g_, sg, ALU.mult)
            dve.wait_ge(E("hist_done"), 1)
            S.sync()
            tt(t1[:, 4:8, SEQ:T], ysmp, bank[6][:, 0:CC * NS].rearrange("p (c b) -> p c b", c=CC), ALU.add, E("cn_r"))
            dve.wait_ge(E("on_sum"), 1)
            dve.wait_ge(E("os_copied"), 2)
            for i in range(3):
                c = slice(OW * i, OW * (i + 1))
                stt(flat[:, c], bank[i][:, 0:OW], -1.0 / DV, flat[:, c], ALU.mult, ALU.add,
                    E("on_c") if i == 2 else None)
            dve.wait_ge(E("cn_sum"), 1)
            stt(t1[:, 4:8, :], bank[3][:, 0:T].unsqueeze(1).broadcast_to([P, CC, T]), -1.0 / FF, t1[:, 4:8, :],
                ALU.mult, ALU.add, E("cn_c"))
            dve.wait_ge(E("on_std"), 3)
            S(v.reciprocal(t2[:, 0:4, :], t2[:, 0:4, :]))
            S.sync()
            tt(t1[:, 0:4, :], t1[:, 0:4, :], t2[:, 0:4, :], ALU.mult)
            S.sync()
            tt(acc[:, 0:4, :], t1[:, 0:4, :], g_, ALU.mult)
            dve.wait_ge(E("cn_std"), 1)
            S(v.reciprocal(stat[:, :], stat[:, :]))
            S.sync()
            tt(t1[:, 4:8, :], t1[:, 4:8, :], stat[:, :].unsqueeze(1).broadcast_to([P, CC, T]), ALU.mult, E("cn_hat"))
            S.sync()
            for c in range(CC):
                ts(acc[:, 4 + c, :], t1[:, 4 + c, :], vec[:, V_CLG + c:V_CLG + c + 1],
                   vec[:, V_CLB + c:V_CLB + c + 1], ALU.mult, ALU.add)
            dve.wait_ge(E("cn_sig"), CC)
            S.sync()
            tt(acc[:, 4:8, :], acc[:, 4:8, :], t2[:, 4:8, :], ALU.mult, E("out0_src"))

            def projected(name, s):
                for m in range(KD):
                    dve.wait_ge(E(name + "_done"), m + 1)
                    residual(s, m, bank[m % 4][:, 0:T], E(name + "_taken"))
                residual_samples(E("ln_r"))

            ada_copy(2)
            projected("out0", 0)
            layer_norm(0)
            modulate(1, E("tm_src"))
            ada_copy(3)

            def token_major(use, dst):
                for t in range(TT):
                    n = min(P, T - t * P)
                    dve.wait_ge(E("tm_tr"), 6 * use + 2 * t + 2)
                    S(v.tensor_copy(dst[0:n, t, 512:1024], bank[2 * t + 1][0:n, :]), E("tm_d"))

            def first_of(out, eq, top):
                S.sync()
                tt(eq, eq, con[:, K_DESC:K_DESC + 4].unsqueeze(1).broadcast_to([P, TT, 4]), ALU.mult)
                S.sync()
                S(v.tensor_reduce(top, eq, AX_X, ALU.max))
                S.sync()
                tt(out, eq, top.broadcast_to([P, TT, 4]), ALU.is_equal)

            def routing(l):
                wide = lambda ap: ap.broadcast_to([P, TT, 4])
                d1, e1, eq, grp, fs, d2, e2, b1, f2, b2, num = small[0:11]
                mx, sm, top, m1, m2, den, r1, r2 = one
                dve.wait_ge(E("route_lg"), l + 1)
                S(v.tensor_reduce(mx, lg[:, :, 0:4], AX_X, ALU.max))
                S.sync()
                tt(d1, lg[:, :, 0:4], wide(mx), ALU.subtract, E("route_d1"))
                S.sync()
                one_op(eq, d1, 0.0, ALU.is_ge)
                first_of(grp, eq, top)
                S.sync()
                fine = lg[:, :, 4:20].rearrange("p t (g e) -> p t g e", g=4)
                pr = prod.rearrange("p t (g e) -> p t g e", g=4)
                for t in range(TT):
                    tt(pr[:, t], fine[:, t], grp[:, t].unsqueeze(2).broadcast_to([P, 4, 4]), ALU.mult)
                S.sync()
                for t in range(TT):
                    S(v.tensor_reduce(fs[:, t], pr[:, t].rearrange("p g e -> p e g"), AX_X, ALU.add))
                S.sync()
                S(v.tensor_reduce(m1, fs, AX_X, ALU.max))
                S.sync()
                tt(d2, fs, wide(m1), ALU.subtract, E("route_d2"))
                S.sync()
                one_op(eq, d2, 0.0, ALU.is_ge)
                first_of(b1, eq, top)
                S.sync()
                stt(f2, b1, -FAR, d2, ALU.mult, ALU.add)
                S.sync()
                S(v.tensor_reduce(m2, f2, AX_X, ALU.max))
                S.sync()
                tt(eq, f2, wide(m2), ALU.is_equal)
                first_of(b2, eq, top)
                dve.wait_ge(E("route_e1"), l + 1)
                S(v.tensor_reduce(sm, e1, AX_X, ALU.add))
                dve.wait_ge(E("route_e2"), l + 1)
                S.sync()
                tt(num, b1, b2, ALU.add)
                S.sync()
                tt(num, num, e2, ALU.mult)
                S.sync()
                S(v.tensor_reduce(den, num, AX_X, ALU.add))
                S.sync()
                tt(den, den, sm, ALU.mult)
                S.sync()
                S(v.reciprocal(den, den))
                S.sync()
                tt(num, num, wide(den), ALU.mult)
                S.sync()
                w = wsel.rearrange("p (i t) -> p i t", i=2)
                for i, b in enumerate((b1, b2)):
                    tt(eq, num, b, ALU.mult)
                    S.sync()
                    S(v.tensor_reduce(w[:, i, :], eq, AX_X, ALU.add))
                    S.sync()
                for i, b in enumerate((b1, b2)):
                    for t in range(TT):
                        tt(pick[i][:, t].rearrange("p (g e) -> p g e", g=4), grp[:, t].unsqueeze(2).broadcast_to([P, 4, 4]),
                           b[:, t].unsqueeze(1).broadcast_to([P, 4, 4]), ALU.mult)
                S.sync()
                tt(mask, pick[0], pick[1], ALU.add)
                S.sync()
                tt(mask, mask, con[:, K_VALID:K_VALID + TT].unsqueeze(2).broadcast_to([P, TT, EXPERTS]), ALU.mult,
                   E("route_mask"))
                dve.wait_ge(E("route_ranks"), l + 1)
                S(v.tensor_copy(rank, bank[7][:, 0:TT * EXPERTS].rearrange("p (t n) -> p t n", t=TT)))
                S(v.tensor_copy(cnt, bank[7][:, TT * EXPERTS:(TT + 1) * EXPERTS]), E("rank_copied"))
                S.sync()
                ts(nch, cnt, float(C), 1.0, ALU.is_gt, ALU.add)
                for j in range(2, (T + C - 1) // C):
                    S.sync()
                    stt(nch, cnt, float(C * j), nch, ALU.is_gt, ALU.add)
                S.sync()
                S(v.tensor_tensor_scan(incl, onef[:, :], nch, 0.0, ALU.mult, ALU.add))
                S.sync()
                S(v.memset(tabf[:, 0:1], 0.0))
                S(v.tensor_copy(tabf[:, 1:EXPERTS + 1], incl))
                S.sync()
                S(v.tensor_copy(tab[l][:, :], tabf), M[l]["table_ready"])
                tt(cnt, incl, nch, ALU.subtract)
                S.sync()
                one_op(cnt, cnt, float(C), ALU.mult)
                S.sync()
                tt(rank, rank, cnt.unsqueeze(1).broadcast_to([P, TT, EXPERTS]), ALU.add)
                S.sync()
                gs = gslot.rearrange("p (i t) -> p i t", i=2)
                for i in range(2):
                    tt((prod, prod2)[i], rank, pick[i], ALU.mult)
                S.sync()
                for i in range(2):
                    S(v.tensor_reduce(gs[:, i, :], (prod, prod2)[i], AX_X, ALU.add))
                S.sync()

            def moe(l):
                m = M[l]
                GU, YT, ST, SC = bank[1], bank[4], bank[5], (bank[6], bank[7])
                flat = lambda ap: ap.rearrange("p k n -> p (k n)")
                gs = gslot.rearrange("p (i t) -> p i t", i=2)

                def hot_rows():
                    for i in range(2):
                        last = v.tensor_tensor(hot[i], iota.unsqueeze(1).broadcast_to([P, TT, C]),
                                               gs[:, i, :].unsqueeze(2).broadcast_to([P, TT, C]), ALU.is_equal)
                    last.then_inc(m["hot_ready"], 1)

                def move_slots():
                    v.tensor_scalar(gslot, gslot, -float(C), None, ALU.add).then_inc(m["slots_moved"], 1)

                def add(f):
                    return v.tensor_tensor(acc[:, f, :], acc[:, f, :], SC[f % 2][:, 0:T], ALU.add)\
                        .then_inc(m["scatter_adds"], 1)

                for f in range(KD):
                    v.memset(acc[:, f, :], 0.0).then_inc(m["scatter_adds"], 1)
                dve.sem_inc(m["hid_done"], 1)
                v.memset(sct, 0.0).then_inc(m["sct_copied"], 1)
                v.memset(ytm[:, 512:1024], 0.0).then_inc(m["yt_copied_d"], 1)
                v.memset(hg_pad, 0.0)
                v.memset(sel_pad, 0.0)
                S(v.memset(ytm[:, 0:512], 0.0), m["zeroed"])
                hot_rows()
                dve.wait_ge(m["hot_ready"], 1)
                move_slots()
                dve.wait_ge(m["selw_ready"], 1)
                dve.wait_ge(m["slots_moved"], 1)
                hot_rows()
                dve.wait_ge(m["hot_ready"], 2)
                move_slots()
                total = dve.value_load(tab[l][0:1, EXPERTS:EXPERTS + 1], min_val=EXPERTS, max_val=MAXCH)
                S.sync()
                with dve.Fori(0, total) as g:
                    g1, g2, g3 = dve.snap(g + 1), dve.snap(g + 2), dve.snap(g + 3)
                    g8 = [dve.snap(g * KD + f) for f in range(KD + 1)]
                    added = dve.snap((g + 1) * KD)
                    dve.wait_ge(m["sig_done"], g1)
                    v.tensor_tensor(flat(sig), flat(sig), GU[:, 0:KF * C], ALU.mult).then_inc(m["t_done"], 1)
                    dve.wait_ge(m["t_done"], g1)
                    v.tensor_tensor(hid, flat(sig), GU[:, KF * C:2 * KF * C], ALU.mult)\
                        .then_inc(m["hid_done"], 1)
                    dve.wait_ge(m["scatter_adds"], added)
                    for f in range(KD):
                        dve.wait_ge(m["scatter_products"], g8[f + 1])
                        add(f)
                    dve.wait_ge(m["down_done"], g1)
                    v.tensor_copy(ytm[0:C, 512:1024], YT[0:C, :]).then_inc(m["yt_copied_d"], 1)
                    dve.wait_ge(m["selwt_done"], g2)
                    v.tensor_copy(sct[0:C, :], ST[0:C, 0:T]).then_inc(m["sct_copied"], 1)
                    dve.wait_ge(m["selw_ready"], g2)
                    dve.wait_ge(m["slots_moved"], g2)
                    hot_rows()
                    dve.wait_ge(m["hot_ready"], g3)
                    move_slots()
                t8 = [dve.snap(total * KD + f) for f in range(KD + 1)]
                end = dve.snap(total + 1)
                dve.wait_ge(m["selw_ready"], end)
                dve.wait_ge(m["hg_copied"], end)
                added = dve.snap((total + 1) * KD)
                dve.wait_ge(m["scatter_adds"], added)
                for f in range(KD):
                    dve.wait_ge(m["scatter_products"], t8[f + 1])
                    add(f)
                dve.wait_ge(m["scatter_adds"], dve.snap((total + 2) * KD))

            def moe_and_residual(l):
                moe(l)
                for f in range(KD):
                    residual(2 * l + 1, f, acc[:, f, :])
                residual_samples(E("ln_r"))

            dve.wait_ge(E("mix0_stored"), 1)
            S(v.memset(lg[:, 2, :], 0.0), E("logits_zeroed"))
            routing(0)
            token_major(0, htm)
            moe_and_residual(0)
            layer_norm(1)
            modulate(2, E("pool_src"))

            S(v.memset(pa[:, :, 0:16], 0.0))
            S(v.memset(pb[:, :, 0:16], 0.0))
            S(v.tensor_copy(pa[:, :, 16:PW], h[:, :, 0:SEQ]))
            src, dst = pa, pb
            for i in range(4):
                S.sync()
                w = 2 ** i
                tt(dst[:, 2 * i:KD, 16:PW], src[:, 2 * i:KD, 16:PW], src[:, 2 * i:KD, 16 - w:PW - w], ALU.add)
                src, dst = dst, src
            S.sync()
            for g in range(4):
                ws = (pb, pa)[g % 2][:, 2 * g:2 * g + 2, 16:PW]
                rc = con[:, K_RCNT + SEQ * g:K_RCNT + SEQ * (g + 1)].unsqueeze(1).broadcast_to([P, 2, SEQ])
                tt(ws, ws, rc, ALU.mult)
            S.sync()
            for g in range(4):
                ws = (pb, pa)[g % 2][:, 2 * g:2 * g + 2, 16:PW]
                tt(t1[:, 2 * g:2 * g + 2, 0:SEQ], ws, h[:, 2 * g:2 * g + 2, 0:SEQ], ALU.subtract)
            dve.wait_ge(E("pool_hist_done"), 1)
            tt(psmp, h[:, :, SEQ:T], bank[6][:, 0:KD * NS].rearrange("p (k b) -> p k b", k=KD), ALU.add)
            S.sync()
            for g, w in enumerate(WINDOWS):
                stt(t1[:, 2 * g:2 * g + 2, SEQ:T], psmp[:, 2 * g:2 * g + 2, :], 1.0 / w, h[:, 2 * g:2 * g + 2, SEQ:T],
                    ALU.mult, ALU.subtract, E("pooled") if g == 3 else None)
            projected("out1", 2)
            layer_norm(2)
            modulate(3, E("tm_src"))
            S(v.memset(lg[:, 2, :], 0.0), E("logits_zeroed"))
            routing(1)
            token_major(1, htm)
            moe_and_residual(1)
            layer_norm(3)
            S.sync()
            S(v.memset(epsb[:, :], EPS), E("tm_src"))
            token_major(2, outb)

        @block.gpsimd
        def _(pool):
            v = nc.gpsimd

            def store(dst, src):
                stores[0] += 1
                pool.dma_start(dst, src).then_inc(s_out, 16)

            stores = [0]
            pool.dma_start(walr, w_in[:, zcols["alr"]:zcols["alr"] + 16].rearrange("(k p) n -> p k n", p=P))\
                .then_inc(s_small, 16)
            pool.dma_start(wa2[0:16, :], I["w_a2"][0]).then_inc(s_small, 16)
            for i in range(2):
                pool.dma_start(conv_prod[0:4 * HIST, i, :],
                               I["state_conv"][0, 4 * i:4 * i + 4].rearrange("b j c -> (b j) c")).then_inc(s_small, 16)
            for i in range(4):
                pool.dma_start(wrep[HIST * i:HIST * (i + 1), :], I["conv_w"][0, 0:HIST, :]).then_inc(s_small, 16)
            for l in range(2):
                pool.dma_start(wr[:, l, :, 0:4], I["w_coarse"][l].rearrange("(k p) n -> p k n", p=P))\
                    .then_inc(s_mix1, 16)
                for g in range(4):
                    pool.dma_start(wr[:, l, :, 4 + 4 * g:8 + 4 * g],
                                   I["w_fine"][l, g].rearrange("(k p) n -> p k n", p=P)).then_inc(s_mix1, 16)
                pool.dma_start(br[0:1, l, 0:4], I["b_coarse"][l:l + 1, :]).then_inc(s_mix1, 16)
                pool.dma_start(br[0:1, l, 4:20], I["b_fine"][l:l + 1].rearrange("l g e -> l (g e)"))\
                    .then_inc(s_mix1, 16)
            store(O[6][0, :, 0:HIST - 1, :], I["state_conv"][0, :, 1:HIST, :])
            store(O[7][0, :, 0:PBUF - 1, :], I["state_pool"][0, :, 1:PBUF, :])
            pool.wait_ge(E("x_copied"), KD)
            st4 = state.rearrange("p b (a n) -> p b a n", a=2)
            for a in range(2):
                pool.dma_start(st4[:, :, a, :], I["state_gla"][0, :, 2 * a:2 * a + 2].rearrange("b h k v -> (h k) b v"))\
                    .then_inc(s_state, 16)
            pool.wait_ge(E("gfin_copied"), 1)
            for a in range(2):
                store(O[2][0, 0, 2 * a:2 * a + 2].rearrange("h k v -> (h k) v"), gfin[:, a, :])
            pool.wait_ge(E("state_new"), 1)
            for a in range(2):
                store(O[5][0, :, 2 * a:2 * a + 2].rearrange("b h k v -> (h k) b v"), st4[:, :, a, :])
            pool.wait_ge(E("conv_rows_copied"), 1)
            store(O[3][0, 0], conv_rows[0:HIST, :])
            store(O[6][0, :, HIST - 1, :], conv_rows[HIST:HIST + NS, :])
            pool.wait_ge(s_out, 16 * stores[0])
            pool.nop().then_inc(E("mix0_stored"), 1)

            def moe(l):
                m = M[l]
                flat = lambda ap: ap.rearrange("p k n -> p (k n)")
                w = wsel.rearrange("p (i t) -> p i t", i=2)
                pool.wait_ge(m["table_ready"], 1)
                total = pool.value_load(tab[l][0:1, EXPERTS:EXPERTS + 1], min_val=EXPERTS, max_val=MAXCH)
                end = pool.snap(total + 1)
                with pool.Fori(0, end) as g:
                    g1 = pool.snap(g + 1)
                    w1, w2 = pool.snap(g * 2 + 1), pool.snap(g * 2 + 2)
                    pool.wait_ge(m["hot_ready"], g1)
                    pool.wait_ge(m["gather_done"], g1)
                    v.tensor_tensor(sel, flat(hot[0]), flat(hot[1]), ALU.add).then_inc(m["sel_ready"], 1)
                    pool.wait_ge(m["sel_ready"], g1)
                    for i in range(2):
                        v.tensor_tensor(hot[i], hot[i], w[:, i, :].unsqueeze(2).broadcast_to([P, TT, C]), ALU.mult)\
                            .then_inc(m["hot_weighted"], 1)
                    pool.wait_ge(m["hot_weighted"], w2)
                    pool.wait_ge(m["selwt_done"], g1)
                    v.tensor_tensor(flat(selw), flat(hot[0]), flat(hot[1]), ALU.add).then_inc(m["selw_ready"], 1)

            moe(0)
            pool.wait_ge(E("ln_r"), 2)
            pool.dma_start(wgrp, I["w_grp_pool"][0].rearrange("g (c p) n -> p g c n", p=P)).then_inc(s_hist, 16)
            pool.dma_start(pbuf[0:NS * PBUF, :], I["state_pool"][0].rearrange("b j d -> (b j) d")).then_inc(s_hist, 16)
            pool.wait_ge(E("prow_copied"), 2)
            store(O[4][0, 0], prow[0:PBUF, :])
            store(O[7][0, :, PBUF - 1, :], prow[PBUF:PBUF + NS, :])
            moe(1)
            for t in range(TT):
                pool.wait_ge(E("tm_a"), 2 * TT + t + 1)
                pool.wait_ge(E("tm_d"), 2 * TT + t + 1)
                if t < 2:
                    store(O[0][0, P * t:P * (t + 1), :], outb[:, t, :])
                else:
                    store(O[1][:, 0, :], outb[0:NS, t, :])
            pool.wait_ge(s_out, 16 * stores[0])


_INS = ["x_prompt", "x_sample", "state_gla", "state_conv", "state_pool", "c_prompt", "c_sample", "w_ada", "b_ada",
        "ln_g", "ln_b", "w_in_even", "w_a2", "b_a", "gla_norm_g", "conv_w", "conv_b", "conv_ln_g", "conv_ln_b",
        "w_out_even", "w_grp_pool", "pool_scale", "w_out_odd", "w_coarse", "b_coarse", "w_fine", "b_fine",
        "w_gate", "w_up", "w_down"]
_OUTS = [(1, SEQ, D), (NS, 1, D), (1, 1, HEADS, DK, DV), (1, 1, HIST, FF), (1, 1, PBUF, D),
         (1, NS, HEADS, DK, DV), (1, NS, HIST, FF), (1, NS, PBUF, D)]


def kernel(**inputs):
    import concourse.bacc as bacc
    from concourse.bass_utils import run_bass_kernel_spmd as run

    nc = bacc.Bacc("TRN2", target_bir_lowering=False, num_devices=1)
    arrays, ins = {}, {}
    for name in _INS:
        arrays["in_" + name] = np.ascontiguousarray(inputs[name])
    arrays["in_shape_constants"] = shape_constants()
    for name, a in arrays.items():
        ins[name[3:]] = nc.dram_tensor(name, a.shape, mybir.dt.from_np(a.dtype), kind="ExternalInput").ap()
    outs = [nc.dram_tensor(f"out_{i}", s, F32, kind="ExternalOutput").ap() for i, s in enumerate(_OUTS)]
    build(nc, ins, outs)
    r = run(nc, [arrays], core_ids=[0])
    return tuple(r.results[0][f"out_{i}"] for i in range(len(_OUTS)))
```
